# Optimizing a Trainium2 kernel written in Bass

```python
import jax, jax.numpy as jnp
from jax import lax
import numpy as np

D_MODEL = 2048
BATCH = 1
SEQ = 256
DEPTH = 1

D_MIX = D_MODEL
D_CONV = D_MIX // 2
CONV_HEADS = 16
D_POOL = D_MIX - D_CONV
POOL_WINDOWS = (2, 4, 8, 16)
N_POOL_GROUPS = len(POOL_WINDOWS)
POOL_GROUP_DIM = D_POOL // N_POOL_GROUPS
CONV_WIDTH = 3
D_IN_PROJ = 3 * D_CONV + D_POOL
D_FF = 4 * D_MODEL
EPS = 1e-6

kernel_name = "hybrid_shortconv_pool_sqrelu_trunk"

def _rmsnorm(x, g):
    xf = x.astype(jnp.float32)
    r = lax.rsqrt(jnp.mean(xf * xf, axis=-1, keepdims=True) + EPS)
    return (xf * r).astype(x.dtype) * g

def _short_conv_mixer(b, c, xt, conv_w):
    u = c * xt
    s = u.shape[1]
    u_pad = jnp.pad(u, ((0, 0), (CONV_WIDTH - 1, 0), (0, 0)))
    conv = conv_w[0] * u_pad[:, 0:s] + conv_w[1] * u_pad[:, 1:s + 1] + conv_w[2] * u_pad[:, 2:s + 2]
    return b * conv

def _pool_mixer(v, pool_w, pool_scale):
    bsz, s, _ = v.shape
    vg = v.reshape(bsz, s, N_POOL_GROUPS, POOL_GROUP_DIM)
    csum = jnp.cumsum(vg.astype(jnp.float32), axis=1)
    pos = jnp.arange(s, dtype=jnp.float32)
    outs = []
    for g, w in enumerate(POOL_WINDOWS):
        cs = csum[:, :, g]
        lagged = jnp.pad(cs[:, :s - w], ((0, 0), (w, 0), (0, 0)))
        count = jnp.minimum(pos + 1.0, float(w))[None, :, None]
        mean = (cs - lagged) / count
        outs.append(mean.astype(v.dtype) - vg[:, :, g])
    d = jnp.stack(outs, axis=2)
    y = jnp.einsum('bsgc,gcd->bsgd', d, pool_w).reshape(bsz, s, D_POOL)
    return y * pool_scale

def setup_inputs(seed: int = 0) -> dict:
    key = jax.random.key(seed)
    ks = jax.random.split(key, 12)
    f32 = jnp.float32
    x = jax.random.normal(ks[0], (BATCH, SEQ, D_MODEL), f32)
    w_in = jax.random.normal(ks[1], (DEPTH, D_MODEL, D_IN_PROJ), f32) * D_MODEL ** -0.5
    conv_w = jax.random.normal(ks[2], (DEPTH, CONV_WIDTH, D_CONV), f32) * CONV_WIDTH ** -0.5
    pool_w = jax.random.normal(ks[3], (DEPTH, N_POOL_GROUPS, POOL_GROUP_DIM, POOL_GROUP_DIM), f32) * POOL_GROUP_DIM ** -0.5
    pool_scale = 1.0 + 0.1 * jax.random.normal(ks[4], (DEPTH, D_POOL), f32)
    w_out = jax.random.normal(ks[5], (DEPTH, D_MIX, D_MODEL), f32) * D_MIX ** -0.5
    norm_mix = 1.0 + 0.05 * jax.random.normal(ks[6], (DEPTH, D_MODEL), f32)
    norm_mlp = 1.0 + 0.05 * jax.random.normal(ks[7], (DEPTH, D_MODEL), f32)
    w_up = jax.random.normal(ks[8], (DEPTH, D_MODEL, D_FF), f32) * D_MODEL ** -0.5
    w_down = jax.random.normal(ks[9], (DEPTH, D_FF, D_MODEL), f32) * D_FF ** -0.5
    norm_final = 1.0 + 0.05 * jax.random.normal(ks[10], (D_MODEL,), f32)
    return {"x": x, "w_in": w_in, "conv_w": conv_w, "pool_w": pool_w, "pool_scale": pool_scale,
            "w_out": w_out, "norm_mix": norm_mix, "norm_mlp": norm_mlp, "w_up": w_up,
            "w_down": w_down, "norm_final": norm_final}

def reference(x, w_in, conv_w, pool_w, pool_scale, w_out, norm_mix, norm_mlp, w_up, w_down, norm_final):
    for l in range(DEPTH):
        h = _rmsnorm(x, norm_mix[l])
        proj = jnp.einsum('bsd,de->bse', h, w_in[l])
        b = proj[..., 0:D_CONV]
        c = proj[..., D_CONV:2 * D_CONV]
        xt = proj[..., 2 * D_CONV:3 * D_CONV]
        v = proj[..., 3 * D_CONV:]
        y_conv = _short_conv_mixer(b, c, xt, conv_w[l])
        y_pool = _pool_mixer(v, pool_w[l], pool_scale[l])
        y = jnp.concatenate([y_conv, y_pool], axis=-1)
        x = x + jnp.einsum('bse,ed->bsd', y, w_out[l])
        h = _rmsnorm(x, norm_mlp[l])
        u = jax.nn.relu(jnp.einsum('bsd,df->bsf', h, w_up[l]))
        x = x + jnp.einsum('bsf,fd->bsd', u * u, w_down[l])
    return _rmsnorm(x, norm_final)


_drawn_inputs = setup_inputs


def setup_inputs(seed=0):
    import zlib

    import numpy as np

    out = dict(_drawn_inputs(seed))
    spreads = {}
    factors = {}
    for name, (base, spread) in spreads.items():
        noise = np.random.default_rng([zlib.crc32(name.encode()), seed]).standard_normal(out[name].shape)
        drawn = base * np.exp(spread * noise) if base else spread * noise
        out[name] = __import__('jax').numpy.asarray(drawn.astype(out[name].dtype))
    for name, factor in factors.items():
        out[name] = (out[name] * factor).astype(out[name].dtype)
    return out
```

```python
import concourse.bass as bass
from concourse import mybir
from contextlib import ExitStack
import numpy as np

D = 2048
S = 256
P = 128
D_CONV = D_POOL = D // 2
WINDOWS = (2, 4, 8, 16)
GROUP = D_POOL // len(WINDOWS)
D_FF = 4 * D
EPS = 1e-6

KT = D // P
NT = 4
BLOCK_COLS = NT * P
CHUNKS = 4
CK = KT // CHUNKS
CHUNK_W = CK * BLOCK_COLS
IN_BLOCKS = (3 * D_CONV + D_POOL) // BLOCK_COLS
OUT_BLOCKS = D // BLOCK_COLS
PARTS = D_FF // D
PART_BLOCKS = 2 * OUT_BLOCKS
FIRST_OUT = IN_BLOCKS
FIRST_UP = FIRST_OUT + OUT_BLOCKS
BLOCKS = FIRST_UP + PARTS * PART_BLOCKS
POOL_JOBS = 2
POOL_AFTER = 4
PAD = max(WINDOWS) // 2
EDGE = max(WINDOWS)

G_MIX, G_MLP, G_FINAL = 0, KT, 2 * KT
CONV_W = 3 * KT
POOL_SCALE = CONV_W + 3 * (KT // 2)
EDGE_INV = POOL_SCALE + KT // 2
PARAMS = EDGE_INV + len(WINDOWS) * EDGE


def turn(n):
    return n if isinstance(n, int) and n < POOL_AFTER else n + POOL_JOBS


def build(nc, x_t, w_stream, pool_w, params, out):
    F32, F32R = mybir.dt.float32, mybir.dt.float32r
    ALU, ACT = mybir.AluOpType, mybir.ActivationFunctionType

    ctx = ExitStack()
    with ctx:
        def sb(name, shape, dt=F32):
            return ctx.enter_context(nc.sbuf_tensor(name, shape, dt))

        def sem(name):
            return ctx.enter_context(nc.semaphore(name))

        w_raw = sb("w_raw", [P, CHUNKS, CHUNK_W])
        w_hi = sb("w_hi", [P, CHUNKS, CHUNK_W], F32R)
        w_lo = sb("w_lo", [P, CHUNKS, CHUNK_W], F32R)
        x = sb("x", [P, KT, S])
        act_a = sb("act_a", [P, KT, 2 * S], F32R)
        act_b = sb("act_b", [P, KT, 2 * S], F32R)
        v_mem = sb("v_mem", [P, (KT // 2) * (PAD + S)])
        c_mem = sb("c_mem", [P, (KT // 2) * (2 + S)])
        win = sb("win", [P, 2, 2, PAD + S])
        cross = sb("cross", [P, NT, S])
        val = sb("val", [P, NT, S])
        inv_rms = sb("inv_rms", [P, S])
        mean_of = sb("mean_of", [P, P])
        prm = sb("prm", [P, PARAMS])
        ps = ctx.enter_context(nc.psum_tensor("ps", [P, 2 * NT, 2 * S], F32))

        v = v_mem[:, :].rearrange("p (k s) -> p k s", k=KT // 2)
        conv = v
        squares = v_mem[:, 0:2 * NT * S].rearrange("p (k s) -> p k s", k=2 * NT)
        u = c_mem[:, :].rearrange("p (k s) -> p k s", k=KT // 2)
        pool_raw = c_mem[:, 0:CHUNK_W]
        pool_hi = act_b[:, 8:12, :]
        pool_lo = act_b[:, 12:16, :]

        params_loaded = sem("params_loaded")
        pool_w_loaded = sem("pool_w_loaded")
        x_loaded = [sem(f"x_loaded{c}") for c in range(CHUNKS)]
        piece_loaded = [sem(f"piece_loaded{k}") for k in range(CK - 1)]
        raw_loaded = [sem(f"raw_loaded{c}") for c in range(CHUNKS)]
        piece_hi = sem("piece_hi")
        piece_lo = sem("piece_lo")
        hi_ready = sem("hi_ready")
        lo_ready = sem("lo_ready")
        chunk_used = sem("chunk_used")
        cross_ready = sem("cross_ready")
        summed = sem("summed")
        x_hi_ready = sem("x_hi_ready")
        x_lo_ready = sem("x_lo_ready")
        act_hi_ready = sem("act_hi_ready")
        act_ready = sem("act_ready")
        value_ready = sem("value_ready")
        squares_ready = sem("squares_ready")
        squares_added = sem("squares_added")
        mean_ready = sem("mean_ready")
        rms_ready = sem("rms_ready")
        inv_rms_ready = sem("inv_rms_ready")
        x_updated = sem("x_updated")
        x_scaled = sem("x_scaled")
        normed = sem("normed")
        gated = sem("gated")
        taps = sem("taps")
        window_step = sem("window_step")
        diff_ready = sem("diff_ready")
        diff_hi = sem("diff_hi")
        diff_act = sem("diff_act")
        pool_hi_ready = sem("pool_hi_ready")
        pool_w_ready = sem("pool_w_ready")
        pool_done = sem("pool_done")
        consts_set = sem("consts_set")
        v_pads_zero = sem("v_pads_zero")
        u_pads_zero = sem("u_pads_zero")
        out_ready = sem("out_ready")
        out_stored = sem("out_stored")

        def bank_halves(parity, half):
            return ps[:, NT * parity:NT * parity + NT, half * S:(half + 1) * S]

        def hi(a, k0, k1):
            return a[:, k0:k1, 0:S]

        def lo(a, k0, k1):
            return a[:, k0:k1, S:2 * S]

        def col(c):
            return prm[:, c:c + 1]

        block = ctx.enter_context(nc.Block())

        @block.sync
        def _(sp):
            def load_x(c):
                sp.dma_start(x[:, CK * c:CK * c + CK, :], x_t[:, CK * c:CK * c + CK, :])\
                  .then_inc(x_loaded[c], 16)

            load_x(0)
            for k in range(CK):
                piece = slice(BLOCK_COLS * k, BLOCK_COLS * (k + 1))
                sp.dma_start(w_raw[:, 0, piece], w_stream[0, :, piece])\
                  .then_inc(piece_loaded[k] if k < CK - 1 else raw_loaded[0], 16)
            for c in range(1, CHUNKS):
                load_x(c)
                sp.dma_start(w_raw[:, c, :], w_stream[c, :, :]).then_inc(raw_loaded[c], 16)
            with sp.Fori(1, BLOCKS) as n:
                for c in range(CHUNKS):
                    sp.wait_ge(lo_ready, 4 * n + (c - 3))
                    sp.dma_start(w_raw[:, c, :], w_stream[bass.ds(4 * n + c, 1), :, :]
                                 .rearrange("a p w -> (a p) w")).then_inc(raw_loaded[c], 16)
            for j in range(NT):
                sp.wait_ge(out_ready, j + 1)
                sp.dma_start(out[:, NT * j:NT * j + NT, :], x[:, NT * j:NT * j + NT, :])\
                  .then_inc(out_stored, 16)
            sp.wait_ge(out_stored, 16 * NT)

        @block.gpsimd
        def _(pool):
            pool.memset(mean_of[:, :], 1.0 / D).then_inc(consts_set, 1)
            pool.memset(win[:, :, :, 0:PAD], 0.0).then_inc(consts_set, 1)
            pool.wait_ge(pool_w_ready, 1)
            pool.memset(u[:, :, 0:2], 0.0).then_inc(u_pads_zero, 1)
            pool.wait_ge(inv_rms_ready, 1)
            pool.memset(v[:, :, 0:PAD], 0.0).then_inc(v_pads_zero, 1)

        @block.tensor
        def _(pe):
            def pair(bank, weights_hi, weights_lo, act, first, last):
                if last:
                    pe.matmul(ps[:, bank, 0:S], weights_lo, act[:, 0:S], start=False, stop=False)
                mm = pe.matmul(ps[:, bank, :], weights_hi, act, start=first, stop=last)
                if not last:
                    mm = pe.matmul(ps[:, bank, 0:S], weights_lo, act[:, 0:S], start=False, stop=False)
                return mm

            def products(src, c, k, t, nts=range(NT)):
                kt = CK * c + k
                for nt in nts:
                    at = BLOCK_COLS * k + P * nt
                    mm = pair(NT * (t % 2) + nt, w_hi[:, c, at:at + P], w_lo[:, c, at:at + P],
                              src[:, kt, :], kt == 0, kt == KT - 1)
                return mm

            def gemm_block(n, src, half, acts_before=None, mean_in_last_bank=0):
                if not (isinstance(n, int) and n < 2):
                    pe.wait_ge(summed, turn(n) - 1)
                for c in range(CHUNKS):
                    if acts_before is not None:
                        pe.wait_ge(act_ready, acts_before + (c + 1))
                    pe.wait_ge(lo_ready, 4 * n + (c + 1))
                    for k in range(CK):
                        if mean_in_last_bank and c == 0 and k == 0:
                            products(src, c, k, half, range(NT - 1))
                            pe.wait_ge(rms_ready, mean_in_last_bank)
                            products(src, c, k, half, range(NT - 1, NT))
                        else:
                            mm = products(src, c, k, half)
                    mm.then_inc(chunk_used, 1)

            def mean_square(r, bank):
                pe.wait_ge(squares_added, 3 * (r + 1))
                for q in range(NT):
                    mm = pe.matmul(ps[:, bank, 0:S], mean_of[:, :], squares[:, q, :],
                                   start=(q == 0), stop=(q == NT - 1))
                mm.then_inc(mean_ready, 1)

            def pool_job(j):
                pe.wait_ge(diff_act, 2 * j + 2)
                pe.wait_ge(summed, POOL_AFTER + j - 1)
                for g in (2 * j, 2 * j + 1):
                    for dt in range(2):
                        bank = NT * (j % 2) + 2 * (g % 2) + dt
                        for kc in range(2):
                            at = S * kc + P * dt
                            mm = pair(bank, pool_hi[:, g, at:at + P], pool_lo[:, g, at:at + P],
                                      act_b[:, 2 * g + kc, :], kc == 0, kc == 1)
                mm.then_inc(pool_done, 1)

            for c in range(CHUNKS):
                if c > 0:
                    pe.wait_ge(lo_ready, c + 1)
                for k in range(CK):
                    if c == 0:
                        if k < CK - 1:
                            pe.wait_ge(piece_lo, k + 1)
                        else:
                            pe.wait_ge(lo_ready, 1)
                    pe.wait_ge(x_lo_ready, CK * c + k + 1)
                    mm = products(act_a, c, k, 0)
                mm.then_inc(chunk_used, 1)
            pe.wait_ge(consts_set, 2)
            mean_square(0, 2 * NT - 1)
            gemm_block(1, act_a, 1, mean_in_last_bank=1)
            gemm_block(2, act_a, 0)
            gemm_block(3, act_a, 1)
            pe.wait_ge(pool_w_ready, 1)
            for j in range(POOL_JOBS):
                pool_job(j)
            with pe.Fori(0, 2) as i:
                gemm_block(2 * i + POOL_AFTER, act_a, 0)
                gemm_block(2 * i + (POOL_AFTER + 1), act_a, 1)
            with pe.Fori(0, 2) as i:
                gemm_block(2 * i + FIRST_OUT, act_b, 0, 0)
                gemm_block(2 * i + (FIRST_OUT + 1), act_b, 1, 0)
            gemm_block(FIRST_UP, act_a, 0, 4)
            mean_square(1, 2 * NT - 1)
            gemm_block(FIRST_UP + 1, act_a, 1, mean_in_last_bank=2)
            gemm_block(FIRST_UP + 2, act_a, 0)
            gemm_block(FIRST_UP + 3, act_a, 1)
            with pe.Fori(0, 2) as i:
                gemm_block(2 * i + (FIRST_UP + 4), act_b, 0, 8)
                gemm_block(2 * i + (FIRST_UP + 5), act_b, 1, 8)
            with pe.Fori(1, PARTS) as p:
                with pe.Fori(0, 2) as i:
                    n = 2 * i + PART_BLOCKS * p + FIRST_UP
                    gemm_block(n, act_a, 0)
                    gemm_block(n + 1, act_a, 1)
                with pe.Fori(0, 2) as i:
                    n = 2 * i + PART_BLOCKS * p + (FIRST_UP + 4)
                    gemm_block(n, act_b, 0, 4 * p + 8)
                    gemm_block(n + 1, act_b, 1, 4 * p + 8)
            mean_square(2, 0)

        @block.scalar
        def _(act):
            act.dma_start(prm[:, :], params[:, :]).then_inc(params_loaded, 16)
            act.dma_start(pool_raw, pool_w[:, :]).then_inc(pool_w_loaded, 16)

            def split(n, c):
                act.wait_ge(raw_loaded[c], 16 * n + 16)
                if not (isinstance(n, int) and n == 0):
                    act.wait_ge(chunk_used, 4 * n + (c - 3))
                act.activation(w_hi[:, c, :], w_raw[:, c, :], ACT.Copy).then_inc(hi_ready, 1)

            def take_cross(t, parity):
                if not (isinstance(t, int) and t == 0):
                    act.wait_ge(summed, t)
                act.activation(cross[:, :, :], bank_halves(parity, 1), ACT.Copy).then_inc(cross_ready, 1)

            def take_block(n, parity):
                act.wait_ge(chunk_used, 4 * n + 4)
                take_cross(turn(n), parity)

            def section(n, before_last=None, parity=1):
                for c in range(CHUNKS - 1):
                    split(n, c)
                if before_last:
                    take_block(n - 1, parity)
                    before_last()
                split(n, CHUNKS - 1)

            def nothing():
                pass

            def act_b_hi(values, k0):
                def go():
                    act.wait_ge(value_ready, values)
                    act.activation(hi(act_b, k0, k0 + NT), val[:, :, :], ACT.Copy)\
                       .then_inc(act_hi_ready, 1)
                return go

            def square(r, q):
                if q >= 2:
                    act.wait_ge(squares_added, 3 * r + q - 1)
                at = 0 if q == 0 else NT
                act.activation(squares[:, at:at + NT, :], x[:, NT * q:NT * q + NT, :], ACT.Square)\
                   .then_inc(squares_ready, 1)

            def root(r, bank):
                act.wait_ge(mean_ready, r + 1)
                act.activation(inv_rms[:, :], ps[:, bank, 0:S], ACT.Sqrt, bias=EPS, scale=1.0)\
                   .then_inc(rms_ready, 1)

            def x_tiles(c):
                act.wait_ge(x_loaded[c], 16)
                for k in range(CK * c, CK * c + CK):
                    act.activation(act_a[:, k, 0:S], x[:, k, :], ACT.Copy, scale=col(G_MIX + k))\
                       .then_inc(x_hi_ready, 1)

            act.wait_ge(params_loaded, 16)
            act.wait_ge(x_loaded[0], 16)
            for k in range(CK):
                act.activation(act_a[:, k, 0:S], x[:, k, :], ACT.Copy, scale=col(G_MIX + k))\
                   .then_inc(x_hi_ready, 1)
                piece = slice(BLOCK_COLS * k, BLOCK_COLS * (k + 1))
                act.wait_ge(piece_loaded[k] if k < CK - 1 else raw_loaded[0], 16)
                act.activation(w_hi[:, 0, piece], w_raw[:, 0, piece], ACT.Copy)\
                   .then_inc(piece_hi if k < CK - 1 else hi_ready, 1)
            for c in range(1, CHUNKS):
                x_tiles(c)
                split(0, c)
            act.wait_ge(pool_w_loaded, 16)
            act.activation(pool_hi, pool_raw.rearrange("p (g w) -> p g w", g=4), ACT.Copy)\
               .then_inc(pool_hi_ready, 1)
            for q in range(4):
                square(0, q)

            def diffs(j):
                for g in (2 * j, 2 * j + 1):
                    act.wait_ge(diff_ready, g + 1)
                    act.activation(hi(act_b, 2 * g, 2 * g + 2), val_diff(g), ACT.Copy)\
                       .then_inc(diff_hi, 1)

            def val_diff(g):
                return win[:, g % 2, :, PAD:PAD + S]

            for c in range(CHUNKS - 1):
                split(1, c)
            root(0, 2 * NT - 1)
            take_block(0, 0)
            split(1, CHUNKS - 1)
            diffs(0)
            section(2, nothing, 1)
            diffs(1)
            section(3, nothing, 0)
            for c in range(CHUNKS - 1):
                split(4, c)
            take_block(3, 1)
            for j in range(POOL_JOBS):
                act.wait_ge(pool_done, j + 1)
                take_cross(POOL_AFTER + j, j)
                act.wait_ge(summed, POOL_AFTER + j + 1)
                for i in range(NT):
                    mm = act.activation(act_b[:, NT * j + i, 0:S], val[:, i, :], ACT.Copy,
                                        scale=col(POOL_SCALE + NT * j + i))
                mm.then_inc(act_hi_ready, 1)
                if j == 0:
                    split(4, CHUNKS - 1)
            section(5, nothing, 0)
            section(6, nothing, 1)
            section(7, act_b_hi(1, 8), 0)
            section(8, act_b_hi(2, 12), 1)

            def new_x(j):
                def go():
                    act.wait_ge(x_updated, j + 1)
                    for i in range(NT * j, NT * j + NT):
                        a = act.activation(act_a[:, i, 0:S], x[:, i, :], ACT.Copy,
                                           scale=col(G_MLP + i))
                    a.then_inc(act_hi_ready, 1)
                    square(1, j)
                return go

            for j in range(OUT_BLOCKS):
                section(FIRST_OUT + 1 + j, new_x(j), j % 2)

            def up_down(n, p):
                for j in range(3):
                    section(n + (1 + j), act_b_hi(4 * p + (3 + j), NT * j), j % 2)
                section(n + 4, act_b_hi(4 * p + 6, NT * 3), 1)
                for j in range(3):
                    section(n + (5 + j), nothing, j % 2)

            n = FIRST_UP
            for c in range(CHUNKS - 1):
                split(n + 1, c)
            root(1, 2 * NT - 1)
            take_block(n, 0)
            act_b_hi(3, 0)()
            split(n + 1, CHUNKS - 1)
            for j in range(1, 4):
                section(n + (1 + j), act_b_hi(3 + j, NT * j), j % 2)
            for j in range(3):
                section(n + (5 + j), nothing, j % 2)
            with act.Fori(1, PARTS) as p:
                n = PART_BLOCKS * p + FIRST_UP
                section(n, nothing, 1)
                up_down(n, p)

            for q in range(4):
                if q == 3:
                    take_block(BLOCKS - 1, 1)
                act.wait_ge(x_updated, 4 * PARTS + q + 1)
                square(2, q)
                for i in range(NT * q, NT * q + NT):
                    if i == NT * q:
                        act.wait_ge(squares_ready, 8 + q + 1)
                    a = act.activation(x[:, i, :], x[:, i, :], ACT.Copy, scale=col(G_FINAL + i))
                a.then_inc(x_scaled, 1)
            root(2, 0)

        @block.vector
        def _(dve):
            def split(n, c):
                dve.wait_ge(hi_ready, 4 * n + (c + 1))
                dve.tensor_tensor(out=w_lo[:, c, :], in0=w_raw[:, c, :],
                                  in1=w_hi[:, c, :].bitcast(F32), op=ALU.subtract)\
                   .then_inc(lo_ready, 1)

            def add_halves(t, parity):
                dve.wait_ge(cross_ready, t + 1)
                dve.tensor_tensor(out=val[:, :, :], in0=bank_halves(parity, 0),
                                  in1=cross[:, :, :], op=ALU.add).then_inc(summed, 1)
                dve.wait_ge(summed, t + 1)

            def section(n, before_last=None, parity=1):
                for c in range(CHUNKS - 1):
                    split(n, c)
                if before_last:
                    add_halves(turn(n - 1), parity)
                    before_last()
                split(n, CHUNKS - 1)

            def by_token():
                return inv_rms[:, None, :].to_broadcast([P, NT, S])

            def times_inv_rms(count, to):
                dve.tensor_tensor(out=to, in0=val[:, :, :], in1=by_token(), op=ALU.mult)\
                   .then_inc(normed, 1)
                dve.wait_ge(normed, count)

            def lo_of_val(count, k0):
                dve.wait_ge(act_hi_ready, count)
                dve.tensor_tensor(out=lo(act_b, k0, k0 + NT), in0=val[:, :, :],
                                  in1=hi(act_b, k0, k0 + NT).bitcast(F32), op=ALU.subtract)\
                   .then_inc(act_ready, 1)
                dve.wait_ge(act_ready, count)

            def lo_of_scaled(to, src, c):
                return dve.scalar_tensor_tensor(out=to[:, S:2 * S], in0=src, scalar=col(c),
                                                in1=to[:, 0:S].bitcast(F32),
                                                op0=ALU.mult, op1=ALU.subtract)

            def add_squares(r, q):
                dve.wait_ge(squares_ready, 4 * r + q + 1)
                if q >= 2:
                    dve.wait_ge(squares_added, 3 * r + q - 1)
                if q:
                    dve.tensor_tensor(out=squares[:, 0:NT, :], in0=squares[:, 0:NT, :],
                                      in1=squares[:, NT:2 * NT, :], op=ALU.add)\
                       .then_inc(squares_added, 1)

            def invert(r):
                dve.wait_ge(rms_ready, r + 1)
                dve.reciprocal(inv_rms[:, :], inv_rms[:, :]).then_inc(inv_rms_ready, 1)
                dve.wait_ge(inv_rms_ready, r + 1)

            def x_tile(k):
                dve.wait_ge(x_hi_ready, k + 1)
                lo_of_scaled(act_a[:, k, :], x[:, k, :], G_MIX + k).then_inc(x_lo_ready, 1)

            for k in range(CK):
                x_tile(k)
                piece = slice(BLOCK_COLS * k, BLOCK_COLS * (k + 1))
                if k < CK - 1:
                    dve.wait_ge(piece_hi, k + 1)
                else:
                    dve.wait_ge(hi_ready, 1)
                dve.tensor_tensor(out=w_lo[:, 0, piece], in0=w_raw[:, 0, piece],
                                  in1=w_hi[:, 0, piece].bitcast(F32), op=ALU.subtract)\
                   .then_inc(piece_lo if k < CK - 1 else lo_ready, 1)
            for c in range(1, CHUNKS):
                for k in range(CK * c, CK * c + CK):
                    x_tile(k)
                split(0, c)
            dve.wait_ge(pool_hi_ready, 1)
            dve.tensor_tensor(out=pool_lo, in0=pool_raw.rearrange("p (g w) -> p g w", g=4),
                              in1=pool_hi.bitcast(F32), op=ALU.subtract).then_inc(pool_w_ready, 1)
            for q in range(4):
                add_squares(0, q)

            steps = [0]

            def window(op):
                op.then_inc(window_step, 1)
                steps[0] += 1
                dve.wait_ge(window_step, steps[0])

            def diff(g):
                vg = v[:, 2 * g:2 * g + 2, :]
                src, to = vg, 0
                n_steps = g + 1
                to = (g + 1 + n_steps - 1) % 2
                for i in range(n_steps):
                    shift = 1 << i
                    dst = win[:, to, :, :]
                    window(dve.tensor_tensor(out=dst[:, :, PAD:PAD + S], in0=src[:, :, PAD:PAD + S],
                                             in1=src[:, :, PAD - shift:PAD + S - shift], op=ALU.add))
                    src, to = dst, 1 - to
                d = win[:, g % 2, :, :]
                edge_inv = prm[:, EDGE_INV + EDGE * g:EDGE_INV + EDGE * (g + 1)]
                edge_inv = edge_inv[:, None, :].to_broadcast([P, 2, EDGE])
                window(dve.tensor_tensor(out=d[:, :, PAD:PAD + EDGE], in0=src[:, :, PAD:PAD + EDGE],
                                         in1=edge_inv, op=ALU.mult))
                window(dve.tensor_tensor(out=d[:, :, PAD:PAD + EDGE], in0=d[:, :, PAD:PAD + EDGE],
                                         in1=vg[:, :, PAD:PAD + EDGE], op=ALU.subtract))
                dve.scalar_tensor_tensor(out=d[:, :, PAD + EDGE:PAD + S],
                                         in0=src[:, :, PAD + EDGE:PAD + S],
                                         scalar=1.0 / WINDOWS[g], in1=vg[:, :, PAD + EDGE:PAD + S],
                                         op0=ALU.mult, op1=ALU.subtract).then_inc(diff_ready, 1)
                dve.wait_ge(diff_hi, g + 1)
                dve.tensor_tensor(out=lo(act_b, 2 * g, 2 * g + 2), in0=d[:, :, PAD:PAD + S],
                                  in1=hi(act_b, 2 * g, 2 * g + 2).bitcast(F32), op=ALU.subtract)\
                   .then_inc(diff_act, 1)
                dve.wait_ge(diff_act, g + 1)

            def v_block(j):
                def go():
                    if j == 0:
                        dve.wait_ge(v_pads_zero, 1)
                        dve.wait_ge(consts_set, 2)
                    times_inv_rms(j + 1, v[:, NT * j:NT * j + NT, PAD:PAD + S])
                return go

            for c in range(CHUNKS - 1):
                split(1, c)
            invert(0)
            add_halves(0, 0)
            v_block(0)()
            split(1, CHUNKS - 1)
            diff(0)
            diff(1)
            section(2, v_block(1), 1)
            diff(2)
            diff(3)

            def c_block(j):
                def go():
                    if j == 0:
                        dve.wait_ge(u_pads_zero, 1)
                    times_inv_rms(3 + j, u[:, NT * j:NT * j + NT, 2:2 + S])
                return go

            def xt_block(j):
                def go():
                    times_inv_rms(5 + j, val[:, :, :])
                    uj = u[:, NT * j:NT * j + NT, :]
                    dve.tensor_tensor(out=uj[:, :, 2:2 + S], in0=uj[:, :, 2:2 + S],
                                      in1=val[:, :, :], op=ALU.mult).then_inc(gated, 1)
                    dve.wait_ge(gated, j + 1)
                    for tap in range(3):
                        for i in range(NT * j, NT * j + NT):
                            w = col(CONV_W + (KT // 2) * tap + i)
                            to = conv[:, i, PAD:PAD + S]
                            if tap == 0:
                                op = dve.tensor_scalar(to, u[:, i, 0:S], w, None, op0=ALU.mult)
                            else:
                                op = dve.scalar_tensor_tensor(out=to, in0=u[:, i, tap:tap + S],
                                                              scalar=w, in1=to,
                                                              op0=ALU.mult, op1=ALU.add)
                        op.then_inc(taps, 1)
                        dve.wait_ge(taps, 3 * j + tap + 1)
                return go

            def b_block(j):
                def go():
                    times_inv_rms(7 + j, val[:, :, :])
                    dve.tensor_tensor(out=val[:, :, :], in0=val[:, :, :],
                                      in1=conv[:, NT * j:NT * j + NT, PAD:PAD + S], op=ALU.mult)\
                       .then_inc(value_ready, 1)
                    dve.wait_ge(value_ready, j + 1)
                    lo_of_val(3 + j, 8 + NT * j)
                return go

            section(3, c_block(0), 0)
            for c in range(CHUNKS - 1):
                split(4, c)
            add_halves(turn(3), 1)
            c_block(1)()
            for j in range(POOL_JOBS):
                add_halves(POOL_AFTER + j, j)
                dve.wait_ge(act_hi_ready, j + 1)
                for i in range(NT):
                    op = lo_of_scaled(act_b[:, NT * j + i, :], val[:, i, :],
                                      POOL_SCALE + NT * j + i)
                op.then_inc(act_ready, 1)
                dve.wait_ge(act_ready, j + 1)
                if j == 0:
                    split(4, CHUNKS - 1)
            section(5, xt_block(0), 0)
            section(6, xt_block(1), 1)
            section(7, b_block(0), 0)
            section(8, b_block(1), 1)

            def add_to_x(count, j):
                xj = x[:, NT * j:NT * j + NT, :]
                dve.tensor_tensor(out=xj, in0=xj, in1=val[:, :, :], op=ALU.add)\
                   .then_inc(x_updated, 1)
                dve.wait_ge(x_updated, count)

            def new_x(j):
                def go():
                    add_to_x(j + 1, j)
                    dve.wait_ge(act_hi_ready, 4 + j + 1)
                    for i in range(NT * j, NT * j + NT):
                        op = lo_of_scaled(act_a[:, i, :], x[:, i, :], G_MLP + i)
                    op.then_inc(act_ready, 1)
                    add_squares(1, j)
                return go

            for j in range(OUT_BLOCKS):
                section(FIRST_OUT + 1 + j, new_x(j), j % 2)

            def up(p, j):
                def go():
                    times_inv_rms(4 * p + (9 + j), val[:, :, :])
                    dve.scalar_tensor_tensor(out=val[:, :, :], in0=val[:, :, :], scalar=0.0,
                                             in1=val[:, :, :], op0=ALU.max, op1=ALU.mult)\
                       .then_inc(value_ready, 1)
                    dve.wait_ge(value_ready, 4 * p + (3 + j))
                    lo_of_val(4 * p + (9 + j), NT * j)
                return go

            def down(p, j):
                def go():
                    add_to_x(4 * p + (5 + j), j)
                return go

            n = FIRST_UP
            for c in range(CHUNKS - 1):
                split(n + 1, c)
            invert(1)
            add_halves(turn(n), 0)
            up(0, 0)()
            split(n + 1, CHUNKS - 1)
            for j in range(1, 4):
                section(n + (1 + j), up(0, j), j % 2)
            for j in range(3):
                section(n + (5 + j), down(0, j), j % 2)
            with dve.Fori(1, PARTS) as p:
                n = PART_BLOCKS * p + FIRST_UP
                section(n, down(p - 1, 3), 1)
                for j in range(4):
                    section(n + (1 + j), up(p, j), j % 2)
                for j in range(3):
                    section(n + (5 + j), down(p, j), j % 2)

            for q in range(4):
                if q == 3:
                    add_halves(turn(BLOCKS - 1), 1)
                    add_to_x(4 * PARTS + 4, 3)
                add_squares(2, q)
            invert(2)
            for q in range(4):
                dve.wait_ge(x_scaled, q + 1)
                xq = x[:, NT * q:NT * q + NT, :]
                dve.tensor_tensor(out=xq, in0=xq, in1=by_token(), op=ALU.mult)\
                   .then_inc(out_ready, 1)


def blocks_of(w, order):
    w = w.reshape(CHUNKS, CK, P, -1, BLOCK_COLS)[:, :, :, order]
    return w.transpose(3, 0, 2, 1, 4).reshape(len(order) * CHUNKS, P, CHUNK_W)


def kernel(x, w_in, conv_w, pool_w, pool_scale, w_out, norm_mix, norm_mlp, w_up, w_down, norm_final):
    import concourse.bacc as bacc
    from concourse.bass_utils import run_bass_kernel_spmd

    x, w_in, conv_w, pool_w, pool_scale, w_out, norm_mix, norm_mlp, w_up, w_down, norm_final = (
        np.asarray(a) for a in (x, w_in, conv_w, pool_w, pool_scale, w_out, norm_mix, norm_mlp,
                                w_up, w_down, norm_final))

    def tiles(a):
        return a.reshape(-1, P).T

    stream = [blocks_of(w_in[0], [6, 7, 2, 3, 4, 5, 0, 1])]
    stream.append(blocks_of(np.concatenate([w_out[0][D_CONV:], w_out[0][:D_CONV]]), [0, 1, 2, 3]))
    for p in range(PARTS):
        stream.append(blocks_of(w_up[0][:, D * p:D * (p + 1)], [0, 1, 2, 3]))
        stream.append(blocks_of(w_down[0][D * p:D * (p + 1)], [0, 1, 2, 3]))
    edge_inv = np.array([[1.0 / min(t + 1, w) for t in range(EDGE)] for w in WINDOWS], np.float32)
    arrays = {
        "x_t": np.ascontiguousarray(x[0].T.reshape(KT, P, S).transpose(1, 0, 2)),
        "w_stream": np.concatenate(stream),
        "pool_w": np.ascontiguousarray(
            pool_w[0].reshape(len(WINDOWS), 2, P, GROUP).transpose(2, 0, 1, 3).reshape(P, CHUNK_W)),
        "params": np.ascontiguousarray(np.concatenate(
            [tiles(norm_mix[0]), tiles(norm_mlp[0]), tiles(norm_final),
             tiles(conv_w[0][0]), tiles(conv_w[0][1]), tiles(conv_w[0][2]), tiles(pool_scale[0]),
             np.broadcast_to(edge_inv.reshape(1, -1), (P, edge_inv.size))], axis=1)),
    }
    nc = bacc.Bacc("TRN2", target_bir_lowering=False, num_devices=1)
    F32 = mybir.dt.float32
    ins = [nc.dram_tensor(name, a.shape, F32, kind="ExternalInput").ap() for name, a in arrays.items()]
    out = nc.dram_tensor("out", (P, KT, S), F32, kind="ExternalOutput").ap()
    build(nc, *ins, out)
    r = run_bass_kernel_spmd(nc, [arrays], core_ids=[0])
    got = r.results[0]["out"]
    return np.ascontiguousarray(got.transpose(1, 0, 2).reshape(D, S).T).reshape(1, S, D)
```

```python
import concourse.bass as bass
from concourse import mybir
from contextlib import ExitStack
import numpy as np

D = 2048
S = 256
P = 128
D_CONV = D_POOL = D // 2
WINDOWS = (2, 4, 8, 16)
GROUP = D_POOL // len(WINDOWS)
D_FF = 4 * D
EPS = 1e-6

KT = D // P
NT = 4
BLOCK_COLS = NT * P
CHUNKS = 4
CK = KT // CHUNKS
CHUNK_W = CK * BLOCK_COLS
IN_BLOCKS = (3 * D_CONV + D_POOL) // BLOCK_COLS
OUT_BLOCKS = D // BLOCK_COLS
PARTS = D_FF // D
PART_BLOCKS = 2 * OUT_BLOCKS
FIRST_OUT = IN_BLOCKS
FIRST_UP = FIRST_OUT + OUT_BLOCKS
BLOCKS = FIRST_UP + PARTS * PART_BLOCKS
POOL_JOBS = 2
POOL_AFTER = 6
PAD = max(WINDOWS) // 2
EDGE = max(WINDOWS)

G_MIX, G_MLP, G_FINAL = 0, KT, 2 * KT
CONV_W = 3 * KT
POOL_SCALE = CONV_W + 3 * (KT // 2)
EDGE_INV = POOL_SCALE + KT // 2
PARAMS = EDGE_INV + len(WINDOWS) * EDGE
WARM_UP = 12


def turn(n):
    return n if isinstance(n, int) and n < POOL_AFTER else n + POOL_JOBS


def build(nc, x_t, w_stream, pool_w, params, out):
    F32, F32R = mybir.dt.float32, mybir.dt.float32r
    ALU, ACT = mybir.AluOpType, mybir.ActivationFunctionType

    ctx = ExitStack()
    with ctx:
        def sb(name, shape, dt=F32):
            return ctx.enter_context(nc.sbuf_tensor(name, shape, dt))

        def sem(name):
            return ctx.enter_context(nc.semaphore(name))

        w_raw = sb("w_raw", [P, CHUNKS, CHUNK_W])
        w_hi = sb("w_hi", [P, CHUNKS, CHUNK_W], F32R)
        w_lo = sb("w_lo", [P, CHUNKS, CHUNK_W], F32R)
        x = sb("x", [P, KT, S])
        act_a = sb("act_a", [P, KT, 2 * S], F32R)
        act_b = sb("act_b", [P, KT, 2 * S], F32R)
        v_mem = sb("v_mem", [P, (KT // 2) * (PAD + S)])
        c_mem = sb("c_mem", [P, (KT // 2) * (2 + S)])
        win = sb("win", [P, 2, 2, PAD + S])
        cross = sb("cross", [P, NT, S])
        val = sb("val", [P, NT, S])
        inv_rms = sb("inv_rms", [P, S])
        mean_of = sb("mean_of", [P, P])
        prm = sb("prm", [P, PARAMS])
        ps = ctx.enter_context(nc.psum_tensor("ps", [P, 2 * NT, 2 * S], F32))

        v = v_mem[:, :].rearrange("p (k s) -> p k s", k=KT // 2)
        conv = v
        squares = v_mem[:, 0:2 * NT * S].rearrange("p (k s) -> p k s", k=2 * NT)
        u = c_mem[:, :].rearrange("p (k s) -> p k s", k=KT // 2)
        pool_raw = c_mem[:, 0:CHUNK_W]
        pool_hi = act_b[:, 8:12, :]
        pool_lo = act_b[:, 12:16, :]

        params_loaded = sem("params_loaded")
        pool_w_loaded = sem("pool_w_loaded")
        x_first_loaded = sem("x_first_loaded")
        x_loaded = [sem(f"x_loaded{c}") for c in range(CHUNKS)]
        piece_loaded = [sem(f"piece_loaded{k}") for k in range(KT)]
        raw_loaded = [sem(f"raw_loaded{c}") for c in range(CHUNKS)]
        piece_hi = sem("piece_hi")
        piece_lo = sem("piece_lo")
        hi_ready = sem("hi_ready")
        lo_ready = sem("lo_ready")
        chunk_used = sem("chunk_used")
        cross_ready = sem("cross_ready")
        summed = sem("summed")
        x_hi_ready = sem("x_hi_ready")
        x_lo_ready = sem("x_lo_ready")
        act_hi_ready = sem("act_hi_ready")
        act_ready = sem("act_ready")
        value_ready = sem("value_ready")
        squares_ready = sem("squares_ready")
        squares_added = sem("squares_added")
        squares_folded = sem("squares_folded")
        mean_ready = sem("mean_ready")
        rms_ready = sem("rms_ready")
        newton = sem("newton")
        inv_rms_ready = sem("inv_rms_ready")
        last_tile_done = sem("last_tile_done")
        last_cross = sem("last_cross")
        last_summed = sem("last_summed")
        last_updated = sem("last_updated")
        last_squared = sem("last_squared")
        last_added = sem("last_added")
        x_updated = sem("x_updated")
        x_scaled = sem("x_scaled")
        normed = sem("normed")
        gated = sem("gated")
        taps = sem("taps")
        window_step = sem("window_step")
        diff_ready = sem("diff_ready")
        diff_hi = sem("diff_hi")
        diff_act = sem("diff_act")
        pool_hi_ready = sem("pool_hi_ready")
        pool_w_ready = sem("pool_w_ready")
        pool_done = sem("pool_done")
        consts_set = sem("consts_set")
        v_pads_zero = sem("v_pads_zero")
        u_pads_zero = sem("u_pads_zero")
        out_ready = sem("out_ready")
        out_stored = sem("out_stored")

        def bank_halves(parity, half):
            return ps[:, NT * parity:NT * parity + NT, half * S:(half + 1) * S]

        def hi(a, k0, k1):
            return a[:, k0:k1, 0:S]

        def lo(a, k0, k1):
            return a[:, k0:k1, S:2 * S]

        def col(c):
            return prm[:, c:c + 1]

        def piece(k):
            return slice(BLOCK_COLS * (k % CK), BLOCK_COLS * (k % CK + 1))

        def is_last(k):
            return k % CK == CK - 1

        block = ctx.enter_context(nc.Block())

        @block.sync
        def _(sp):
            def load_x(k0, k1, loaded):
                sp.dma_start(x[:, k0:k1, :], x_t[:, k0:k1, :]).then_inc(loaded, 16)

            for k in range(KT):
                if k == 0:
                    load_x(0, 1, x_first_loaded)
                elif k == 1:
                    load_x(1, CK, x_loaded[0])
                elif k % CK == 0:
                    load_x(k, k + CK, x_loaded[k // CK])
                sp.dma_start(w_raw[:, k // CK, piece(k)], w_stream[k // CK, :, piece(k)])\
                  .then_inc(raw_loaded[k // CK] if is_last(k) else piece_loaded[k], 16)
            with sp.Fori(1, BLOCKS) as n:
                for c in range(CHUNKS):
                    sp.wait_ge(lo_ready, 4 * n + (c - 3))
                    sp.dma_start(w_raw[:, c, :], w_stream[bass.ds(4 * n + c, 1), :, :]
                                 .rearrange("a p w -> (a p) w")).then_inc(raw_loaded[c], 16)
            for j in range(KT // 2):
                sp.wait_ge(out_ready, j + 1)
                sp.dma_start(out[:, 2 * j:2 * j + 2, :], x[:, 2 * j:2 * j + 2, :])\
                  .then_inc(out_stored, 16)
            sp.wait_ge(out_stored, 16 * (KT // 2))

        @block.gpsimd
        def _(pool):
            pool.memset(mean_of[:, :], 1.0 / D).then_inc(consts_set, 1)
            pool.memset(win[:, :, :, 0:PAD], 0.0).then_inc(consts_set, 1)
            pool.wait_ge(pool_w_ready, 1)
            pool.memset(u[:, :, 0:2], 0.0).then_inc(u_pads_zero, 1)
            pool.wait_ge(inv_rms_ready, 1)
            pool.memset(v[:, :, 0:PAD], 0.0).then_inc(v_pads_zero, 1)

        @block.tensor
        def _(pe):
            def pair(bank, weights_hi, weights_lo, act, first, last):
                if last:
                    pe.matmul(ps[:, bank, 0:S], weights_lo, act[:, 0:S], start=False, stop=False)
                mm = pe.matmul(ps[:, bank, :], weights_hi, act, start=first, stop=last)
                if not last:
                    mm = pe.matmul(ps[:, bank, 0:S], weights_lo, act[:, 0:S], start=False, stop=False)
                return mm

            def products(src, c, k, t, nts=range(NT)):
                kt = CK * c + k
                for nt in nts:
                    at = BLOCK_COLS * k + P * nt
                    mm = pair(NT * (t % 2) + nt, w_hi[:, c, at:at + P], w_lo[:, c, at:at + P],
                              src[:, kt, :], kt == 0, kt == KT - 1)
                return mm

            def gemm_block(n, src, half, acts_before=None, norm=None, norm_after=0,
                           chunks=range(CHUNKS), before_pool=False):
                if not (isinstance(n, int) and n < 2):
                    pe.wait_ge(summed, n - 1 if before_pool else turn(n) - 1)
                for c in chunks:
                    if acts_before is not None:
                        pe.wait_ge(act_ready, acts_before + (c + 1))
                    pe.wait_ge(lo_ready, 4 * n + (c + 1))
                    for k in range(CK):
                        mm = products(src, c, k, half)
                        if k == CK - 1:
                            mm.then_inc(chunk_used, 1)
                        if norm is not None and CK * c + k == norm_after:
                            pe.wait_ge(summed, turn(n))
                            mean_square(norm)

            def mean_square(r):
                pe.wait_ge(squares_folded, 2 * r + 2)
                pe.matmul(ps[:, 0, 0:S], mean_of[:, :], squares[:, 0, :],
                          start=True, stop=True).then_inc(mean_ready, 1)

            def pool_job(j):
                pe.wait_ge(diff_act, 2 * j + 2)
                pe.wait_ge(summed, POOL_AFTER + j - 1)
                for g in (2 * j, 2 * j + 1):
                    for dt in range(2):
                        bank = NT * (j % 2) + 2 * (g % 2) + dt
                        for kc in range(2):
                            at = S * kc + P * dt
                            mm = pair(bank, pool_hi[:, g, at:at + P], pool_lo[:, g, at:at + P],
                                      act_b[:, 2 * g + kc, :], kc == 0, kc == 1)
                mm.then_inc(pool_done, 1)

            pe.wait_ge(consts_set, 1)
            for _ in range(WARM_UP):
                pe.matmul(ps[:, 2 * NT - 1, 0:P], mean_of[:, :], mean_of[:, :], start=True, stop=True)
            for k in range(KT):
                if is_last(k):
                    pe.wait_ge(lo_ready, k // CK + 1)
                else:
                    pe.wait_ge(piece_lo, k - k // CK + 1)
                pe.wait_ge(x_lo_ready, k + 1)
                mm = products(act_a, k // CK, k % CK, 0)
                if is_last(k):
                    mm.then_inc(chunk_used, 1)
            pe.wait_ge(consts_set, 2)
            gemm_block(1, act_a, 1, norm=0, norm_after=11)
            pe.wait_ge(inv_rms_ready, 1)
            with pe.Fori(1, POOL_AFTER // 2) as i:
                gemm_block(2 * i, act_a, 0, before_pool=True)
                gemm_block(2 * i + 1, act_a, 1, before_pool=True)
            pe.wait_ge(pool_w_ready, 1)
            for j in range(POOL_JOBS):
                pool_job(j)
            gemm_block(6, act_a, 0)
            gemm_block(7, act_a, 1)
            with pe.Fori(0, 2) as i:
                gemm_block(2 * i + FIRST_OUT, act_b, 0, 0)
                gemm_block(2 * i + (FIRST_OUT + 1), act_b, 1, 0)
            gemm_block(FIRST_UP, act_a, 0, 4)
            gemm_block(FIRST_UP + 1, act_a, 1, norm=1, norm_after=4)
            pe.wait_ge(inv_rms_ready, 2)
            gemm_block(FIRST_UP + 2, act_a, 0)
            gemm_block(FIRST_UP + 3, act_a, 1)
            with pe.Fori(0, 2) as i:
                gemm_block(2 * i + (FIRST_UP + 4), act_b, 0, 8)
                gemm_block(2 * i + (FIRST_UP + 5), act_b, 1, 8)

            def up_pair(n):
                gemm_block(n, act_a, 0)
                gemm_block(n + 1, act_a, 1)

            def down_pair(n, acts_before):
                gemm_block(n, act_b, 0, acts_before)
                gemm_block(n + 1, act_b, 1, acts_before)

            with pe.Fori(1, PARTS - 1) as p:
                with pe.Fori(0, 2) as i:
                    up_pair(2 * i + PART_BLOCKS * p + FIRST_UP)
                with pe.Fori(0, 2) as i:
                    down_pair(2 * i + PART_BLOCKS * p + (FIRST_UP + 4), 4 * p + 8)
            with pe.Fori(0, 2) as i:
                up_pair(2 * i + (BLOCKS - PART_BLOCKS))
            down_pair(BLOCKS - 4, 4 * PARTS + 4)
            gemm_block(BLOCKS - 2, act_b, 0, 4 * PARTS + 4)
            gemm_block(BLOCKS - 1, act_b, 1, 4 * PARTS + 4, chunks=(0, 1))
            for nt in range(NT):
                for c in (2, 3):
                    if nt == 0:
                        pe.wait_ge(act_ready, 4 * PARTS + 4 + (c + 1))
                        pe.wait_ge(lo_ready, 4 * (BLOCKS - 1) + (c + 1))
                    for k in range(CK):
                        mm = products(act_b, c, k, 1, (nt,))
                mm.then_inc(last_tile_done, 1)
            pe.wait_ge(summed, turn(BLOCKS - 2) + 1)
            pe.wait_ge(last_added, NT - 1)
            pe.matmul(ps[:, 0, 0:S], mean_of[:, :], squares[:, 0, :], start=True, stop=False)
            pe.wait_ge(last_squared, NT)
            pe.matmul(ps[:, 0, 0:S], mean_of[:, :], squares[:, 2 * NT - 1, :],
                      start=False, stop=True).then_inc(mean_ready, 1)

        @block.scalar
        def _(act):
            act.dma_start(prm[:, :], params[:, :]).then_inc(params_loaded, 16)

            def split(n, c):
                act.wait_ge(raw_loaded[c], 16 * n + 16)
                if not (isinstance(n, int) and n == 0):
                    act.wait_ge(chunk_used, 4 * n + (c - 3))
                act.activation(w_hi[:, c, :], w_raw[:, c, :], ACT.Copy).then_inc(hi_ready, 1)

            def take_cross(t, parity):
                if not (isinstance(t, int) and t == 0):
                    act.wait_ge(summed, t)
                act.activation(cross[:, :, :], bank_halves(parity, 1), ACT.Copy).then_inc(cross_ready, 1)

            def take_block(n, parity):
                act.wait_ge(chunk_used, 4 * n + 4)
                take_cross(turn(n), parity)

            def section(n, before_last=None, parity=1):
                for c in range(CHUNKS - 1):
                    split(n, c)
                if before_last:
                    take_block(n - 1, parity)
                    before_last()
                split(n, CHUNKS - 1)

            def nothing():
                pass

            def act_b_hi(values, k0):
                def go():
                    act.wait_ge(value_ready, values)
                    act.activation(hi(act_b, k0, k0 + NT), val[:, :, :], ACT.Copy)\
                       .then_inc(act_hi_ready, 1)
                return go

            def square(r, q):
                if q >= 2:
                    act.wait_ge(squares_added, 3 * r + q - 1)
                at = 0 if q == 0 else NT
                act.activation(squares[:, at:at + NT, :], x[:, NT * q:NT * q + NT, :], ACT.Square)\
                   .then_inc(squares_ready, 1)

            def root(r):
                act.wait_ge(mean_ready, r + 1)
                act.activation(inv_rms[:, :], ps[:, 0, 0:S], ACT.Sqrt, bias=EPS, scale=1.0)\
                   .then_inc(rms_ready, 1)

            act.wait_ge(params_loaded, 16)
            for k in range(KT):
                if k == 0:
                    act.wait_ge(x_first_loaded, 16)
                elif k == 1 or k % CK == 0:
                    act.wait_ge(x_loaded[k // CK], 16)
                act.activation(act_a[:, k, 0:S], x[:, k, :], ACT.Copy, scale=col(G_MIX + k))\
                   .then_inc(x_hi_ready, 1)
                act.wait_ge(raw_loaded[k // CK] if is_last(k) else piece_loaded[k], 16)
                act.activation(w_hi[:, k // CK, piece(k)], w_raw[:, k // CK, piece(k)], ACT.Copy)\
                   .then_inc(hi_ready if is_last(k) else piece_hi, 1)
            act.dma_start(pool_raw, pool_w[:, :]).then_inc(pool_w_loaded, 16)
            split(1, 0)
            split(1, 1)
            square(0, 0)
            square(0, 1)
            split(1, 2)
            square(0, 2)
            square(0, 3)
            split(1, 3)

            def diff(g):
                act.wait_ge(diff_ready, g + 1)
                act.activation(hi(act_b, 2 * g, 2 * g + 2), win[:, g % 2, :, PAD:PAD + S], ACT.Copy)\
                   .then_inc(diff_hi, 1)

            take_block(0, 0)
            split(2, 0)
            root(0)
            act.wait_ge(pool_w_loaded, 16)
            act.activation(pool_hi, pool_raw.rearrange("p (g w) -> p g w", g=4), ACT.Copy)\
               .then_inc(pool_hi_ready, 1)
            split(2, 1)
            split(2, 2)
            diff(0)
            take_block(1, 1)
            split(2, 3)
            diff(1)
            split(3, 0)
            split(3, 1)
            diff(2)
            split(3, 2)
            take_block(2, 0)
            split(3, 3)
            section(4, nothing, 1)
            diff(3)
            section(5, nothing, 0)
            for c in range(CHUNKS - 1):
                split(6, c)
            take_block(5, 1)
            for j in range(POOL_JOBS):
                act.wait_ge(pool_done, j + 1)
                take_cross(POOL_AFTER + j, j)
                act.wait_ge(summed, POOL_AFTER + j + 1)
                for i in range(NT):
                    mm = act.activation(act_b[:, NT * j + i, 0:S], val[:, i, :], ACT.Copy,
                                        scale=col(POOL_SCALE + NT * j + i))
                mm.then_inc(act_hi_ready, 1)
                if j == 0:
                    split(6, CHUNKS - 1)
            section(7, act_b_hi(1, 8), 0)
            section(8, act_b_hi(2, 12), 1)

            def new_x(j):
                def go():
                    act.wait_ge(x_updated, j + 1)
                    for i in range(NT * j, NT * j + NT):
                        a = act.activation(act_a[:, i, 0:S], x[:, i, :], ACT.Copy,
                                           scale=col(G_MLP + i))
                    a.then_inc(act_hi_ready, 1)
                    square(1, j)
                return go

            for j in range(OUT_BLOCKS):
                section(FIRST_OUT + 1 + j, new_x(j), j % 2)

            def up_down(n, p):
                for j in range(3):
                    section(n + (1 + j), act_b_hi(4 * p + (3 + j), NT * j), j % 2)
                section(n + 4, act_b_hi(4 * p + 6, NT * 3), 1)
                for j in range(3):
                    section(n + (5 + j), nothing, j % 2)

            n = FIRST_UP
            for c in range(CHUNKS):
                split(n + 1, c)
            take_block(n, 0)
            root(1)
            act_b_hi(3, 0)()
            for j in range(1, 4):
                section(n + (1 + j), act_b_hi(3 + j, NT * j), j % 2)
            for j in range(3):
                section(n + (5 + j), nothing, j % 2)
            with act.Fori(1, PARTS) as p:
                n = PART_BLOCKS * p + FIRST_UP
                section(n, nothing, 1)
                up_down(n, p)

            def scale_x(k0, k1):
                for i in range(k0, k1):
                    a = act.activation(x[:, i, :], x[:, i, :], ACT.Copy, scale=col(G_FINAL + i))
                return a

            for q in range(3):
                act.wait_ge(x_updated, 4 * PARTS + q + 1)
                square(2, q)
                act.wait_ge(squares_ready, 8 + q + 1)
                scale_x(NT * q, NT * q + NT).then_inc(x_scaled, 1)
            act.wait_ge(squares_added, 8)
            for i in range(NT):
                act.wait_ge(last_tile_done, i + 1)
                if i == 0:
                    act.wait_ge(summed, turn(BLOCKS - 1))
                act.activation(cross[:, i, :], ps[:, NT + i, S:2 * S], ACT.Copy)\
                   .then_inc(last_cross, 1)
                act.wait_ge(last_updated, i + 1)
                act.activation(squares[:, NT + i, :], x[:, 3 * NT + i, :], ACT.Square)\
                   .then_inc(last_squared, 1)
            act.wait_ge(last_squared, NT)
            root(2)
            scale_x(3 * NT, KT).then_inc(x_scaled, 1)

        @block.vector
        def _(dve):
            def split(n, c):
                dve.wait_ge(hi_ready, 4 * n + (c + 1))
                dve.tensor_tensor(out=w_lo[:, c, :], in0=w_raw[:, c, :],
                                  in1=w_hi[:, c, :].bitcast(F32), op=ALU.subtract)\
                   .then_inc(lo_ready, 1)

            def add_halves(t, parity):
                dve.wait_ge(cross_ready, t + 1)
                dve.tensor_tensor(out=val[:, :, :], in0=bank_halves(parity, 0),
                                  in1=cross[:, :, :], op=ALU.add).then_inc(summed, 1)
                dve.wait_ge(summed, t + 1)

            def section(n, before_last=None, parity=1):
                for c in range(CHUNKS - 1):
                    split(n, c)
                if before_last:
                    add_halves(turn(n - 1), parity)
                    before_last()
                split(n, CHUNKS - 1)

            def by_token():
                return inv_rms[:, None, :].to_broadcast([P, NT, S])

            def times_inv_rms(count, to):
                dve.tensor_tensor(out=to, in0=val[:, :, :], in1=by_token(), op=ALU.mult)\
                   .then_inc(normed, 1)
                dve.wait_ge(normed, count)

            def lo_of_val(count, k0):
                dve.wait_ge(act_hi_ready, count)
                dve.tensor_tensor(out=lo(act_b, k0, k0 + NT), in0=val[:, :, :],
                                  in1=hi(act_b, k0, k0 + NT).bitcast(F32), op=ALU.subtract)\
                   .then_inc(act_ready, 1)
                dve.wait_ge(act_ready, count)

            def lo_of_scaled(to, src, c):
                return dve.scalar_tensor_tensor(out=to[:, S:2 * S], in0=src, scalar=col(c),
                                                in1=to[:, 0:S].bitcast(F32),
                                                op0=ALU.mult, op1=ALU.subtract)

            def add_squares(r, q):
                dve.wait_ge(squares_ready, 4 * r + q + 1)
                if q >= 2:
                    dve.wait_ge(squares_added, 3 * r + q - 1)
                if q:
                    dve.tensor_tensor(out=squares[:, 0:NT, :], in0=squares[:, 0:NT, :],
                                      in1=squares[:, NT:2 * NT, :], op=ALU.add)\
                       .then_inc(squares_added, 1)

            def fold_squares(r):
                for i, half in enumerate((2, 1)):
                    dve.wait_ge(squares_added, 3 * r + 3 if r < 2 else 8)
                    dve.tensor_tensor(out=squares[:, 0:half, :], in0=squares[:, 0:half, :],
                                      in1=squares[:, half:2 * half, :], op=ALU.add)\
                       .then_inc(squares_folded, 1)
                    dve.wait_ge(squares_folded, 2 * r + i + 1)

            def invert(r):
                tmp, mean = win[:, 0, 0, PAD:PAD + S], ps[:, 0, 0:S]
                dve.wait_ge(rms_ready, r + 1)

                def step(i, op):
                    op.then_inc(newton, 1)
                    dve.wait_ge(newton, 4 * r + i + 1)

                step(0, dve.reciprocal(inv_rms[:, :], inv_rms[:, :]))
                step(1, dve.scalar_tensor_tensor(out=tmp, in0=mean, scalar=EPS, in1=inv_rms[:, :],
                                                 op0=ALU.add, op1=ALU.mult))
                step(2, dve.tensor_tensor(out=tmp, in0=tmp, in1=inv_rms[:, :], op=ALU.mult))
                step(3, dve.tensor_scalar(tmp, tmp, -0.5, 1.5, op0=ALU.mult, op1=ALU.add))
                dve.tensor_tensor(out=inv_rms[:, :], in0=inv_rms[:, :], in1=tmp, op=ALU.mult)\
                   .then_inc(inv_rms_ready, 1)
                dve.wait_ge(inv_rms_ready, r + 1)

            for k in range(KT):
                dve.wait_ge(x_hi_ready, k + 1)
                lo_of_scaled(act_a[:, k, :], x[:, k, :], G_MIX + k).then_inc(x_lo_ready, 1)
                if is_last(k):
                    dve.wait_ge(hi_ready, k // CK + 1)
                else:
                    dve.wait_ge(piece_hi, k - k // CK + 1)
                dve.tensor_tensor(out=w_lo[:, k // CK, piece(k)], in0=w_raw[:, k // CK, piece(k)],
                                  in1=w_hi[:, k // CK, piece(k)].bitcast(F32), op=ALU.subtract)\
                   .then_inc(lo_ready if is_last(k) else piece_lo, 1)
            split(1, 0)
            split(1, 1)
            add_squares(0, 0)
            add_squares(0, 1)
            split(1, 2)
            add_squares(0, 2)
            add_squares(0, 3)
            fold_squares(0)
            split(1, 3)

            steps = [0]

            def window(op):
                op.then_inc(window_step, 1)
                steps[0] += 1
                dve.wait_ge(window_step, steps[0])

            def diff(g):
                vg = v[:, 2 * g:2 * g + 2, :]
                src, to = vg, 0
                n_steps = g + 1
                to = (g + 1 + n_steps - 1) % 2
                for i in range(n_steps):
                    shift = 1 << i
                    dst = win[:, to, :, :]
                    window(dve.tensor_tensor(out=dst[:, :, PAD:PAD + S], in0=src[:, :, PAD:PAD + S],
                                             in1=src[:, :, PAD - shift:PAD + S - shift], op=ALU.add))
                    src, to = dst, 1 - to
                d = win[:, g % 2, :, :]
                edge_inv = prm[:, EDGE_INV + EDGE * g:EDGE_INV + EDGE * (g + 1)]
                edge_inv = edge_inv[:, None, :].to_broadcast([P, 2, EDGE])
                window(dve.tensor_tensor(out=d[:, :, PAD:PAD + EDGE], in0=src[:, :, PAD:PAD + EDGE],
                                         in1=edge_inv, op=ALU.mult))
                window(dve.tensor_tensor(out=d[:, :, PAD:PAD + EDGE], in0=d[:, :, PAD:PAD + EDGE],
                                         in1=vg[:, :, PAD:PAD + EDGE], op=ALU.subtract))
                dve.scalar_tensor_tensor(out=d[:, :, PAD + EDGE:PAD + S],
                                         in0=src[:, :, PAD + EDGE:PAD + S],
                                         scalar=1.0 / WINDOWS[g], in1=vg[:, :, PAD + EDGE:PAD + S],
                                         op0=ALU.mult, op1=ALU.subtract).then_inc(diff_ready, 1)

            def diff_lo(g):
                d = win[:, g % 2, :, :]
                dve.wait_ge(diff_hi, g + 1)
                dve.tensor_tensor(out=lo(act_b, 2 * g, 2 * g + 2), in0=d[:, :, PAD:PAD + S],
                                  in1=hi(act_b, 2 * g, 2 * g + 2).bitcast(F32), op=ALU.subtract)\
                   .then_inc(diff_act, 1)
                dve.wait_ge(diff_act, g + 1)

            def take_v(j):
                times_inv_rms(j + 1, v[:, NT * j:NT * j + NT, PAD:PAD + S])

            add_halves(0, 0)
            split(2, 0)
            dve.wait_ge(consts_set, 2)
            invert(0)
            dve.wait_ge(pool_hi_ready, 1)
            dve.tensor_tensor(out=pool_lo, in0=pool_raw.rearrange("p (g w) -> p g w", g=4),
                              in1=pool_hi.bitcast(F32), op=ALU.subtract).then_inc(pool_w_ready, 1)
            split(2, 1)
            dve.wait_ge(v_pads_zero, 1)
            take_v(0)
            diff(0)
            split(2, 2)
            diff_lo(0)
            add_halves(turn(1), 1)
            take_v(1)
            diff(1)
            split(2, 3)
            diff_lo(1)
            split(3, 0)
            diff(2)
            split(3, 1)
            diff_lo(2)
            split(3, 2)

            def c_block(j):
                def go():
                    if j == 0:
                        dve.wait_ge(u_pads_zero, 1)
                    uj = u[:, NT * j:NT * j + NT, 2:2 + S]
                    times_inv_rms(3 + 2 * j, uj)
                    dve.tensor_tensor(out=uj, in0=uj, in1=by_token(), op=ALU.mult)\
                       .then_inc(normed, 1)
                return go

            def take_xt(j):
                uj = u[:, NT * j:NT * j + NT, 2:2 + S]
                dve.tensor_tensor(out=uj, in0=uj, in1=val[:, :, :], op=ALU.mult).then_inc(gated, 1)
                dve.wait_ge(gated, j + 1)

            def convolve(j):
                for tap in range(3):
                    for i in range(NT * j, NT * j + NT):
                        w = col(CONV_W + (KT // 2) * tap + i)
                        to = conv[:, i, PAD:PAD + S]
                        if tap == 0:
                            op = dve.tensor_scalar(to, u[:, i, 0:S], w, None, op0=ALU.mult)
                        else:
                            op = dve.scalar_tensor_tensor(out=to, in0=u[:, i, tap:tap + S],
                                                          scalar=w, in1=to,
                                                          op0=ALU.mult, op1=ALU.add)
                    op.then_inc(taps, 1)
                    dve.wait_ge(taps, 3 * j + tap + 1)

            def xt_block(j):
                def go():
                    take_xt(j)
                    convolve(j)
                return go

            def b_block(j):
                def go():
                    times_inv_rms(7 + j, val[:, :, :])
                    dve.tensor_tensor(out=val[:, :, :], in0=val[:, :, :],
                                      in1=conv[:, NT * j:NT * j + NT, PAD:PAD + S], op=ALU.mult)\
                       .then_inc(value_ready, 1)
                    dve.wait_ge(value_ready, j + 1)
                    lo_of_val(3 + j, 8 + NT * j)
                return go

            add_halves(turn(2), 0)
            c_block(0)()
            split(3, 3)
            section(4, c_block(1), 1)
            diff(3)
            diff_lo(3)
            section(5, xt_block(0), 0)
            for c in range(CHUNKS - 1):
                split(6, c)
            add_halves(turn(5), 1)
            take_xt(1)
            for j in range(POOL_JOBS):
                add_halves(POOL_AFTER + j, j)
                dve.wait_ge(act_hi_ready, j + 1)
                for i in range(NT):
                    op = lo_of_scaled(act_b[:, NT * j + i, :], val[:, i, :],
                                      POOL_SCALE + NT * j + i)
                op.then_inc(act_ready, 1)
                dve.wait_ge(act_ready, j + 1)
                if j == 0:
                    split(6, CHUNKS - 1)
            convolve(1)
            section(7, b_block(0), 0)
            section(8, b_block(1), 1)

            def add_to_x(count, j):
                xj = x[:, NT * j:NT * j + NT, :]
                dve.tensor_tensor(out=xj, in0=xj, in1=val[:, :, :], op=ALU.add)\
                   .then_inc(x_updated, 1)
                dve.wait_ge(x_updated, count)

            def new_x(j):
                def go():
                    add_to_x(j + 1, j)
                    dve.wait_ge(act_hi_ready, 4 + j + 1)
                    for i in range(NT * j, NT * j + NT):
                        op = lo_of_scaled(act_a[:, i, :], x[:, i, :], G_MLP + i)
                    op.then_inc(act_ready, 1)
                    add_squares(1, j)
                    if j == 3:
                        fold_squares(1)
                return go

            for j in range(OUT_BLOCKS):
                section(FIRST_OUT + 1 + j, new_x(j), j % 2)

            def up(p, j):
                def go():
                    times_inv_rms(4 * p + (9 + j), val[:, :, :])
                    dve.scalar_tensor_tensor(out=val[:, :, :], in0=val[:, :, :], scalar=0.0,
                                             in1=val[:, :, :], op0=ALU.max, op1=ALU.mult)\
                       .then_inc(value_ready, 1)
                    dve.wait_ge(value_ready, 4 * p + (3 + j))
                    lo_of_val(4 * p + (9 + j), NT * j)
                return go

            def down(p, j):
                def go():
                    add_to_x(4 * p + (5 + j), j)
                return go

            n = FIRST_UP
            for c in range(CHUNKS):
                split(n + 1, c)
            add_halves(turn(n), 0)
            invert(1)
            up(0, 0)()
            for j in range(1, 4):
                section(n + (1 + j), up(0, j), j % 2)
            for j in range(3):
                section(n + (5 + j), down(0, j), j % 2)
            with dve.Fori(1, PARTS) as p:
                n = PART_BLOCKS * p + FIRST_UP
                section(n, down(p - 1, 3), 1)
                for j in range(4):
                    section(n + (1 + j), up(p, j), j % 2)
                for j in range(3):
                    section(n + (5 + j), down(p, j), j % 2)

            for q in range(3):
                add_squares(2, q)
            fold_squares(2)
            for i in range(NT):
                dve.wait_ge(last_cross, i + 1)
                dve.tensor_tensor(out=val[:, i, :], in0=ps[:, NT + i, 0:S], in1=cross[:, i, :],
                                  op=ALU.add).then_inc(last_summed, 1)
                dve.wait_ge(last_summed, i + 1)
                xi = x[:, 3 * NT + i, :]
                dve.tensor_tensor(out=xi, in0=xi, in1=val[:, i, :], op=ALU.add)\
                   .then_inc(last_updated, 1)
                if i < NT - 1:
                    dve.wait_ge(last_squared, i + 1)
                    dve.tensor_tensor(out=squares[:, 0, :], in0=squares[:, 0, :],
                                      in1=squares[:, NT + i, :], op=ALU.add)\
                       .then_inc(last_added, 1)
                    dve.wait_ge(last_added, i + 1)
            invert(2)
            for j in range(KT // 2):
                dve.wait_ge(x_scaled, j // 2 + 1)
                xj = x[:, 2 * j:2 * j + 2, :]
                dve.tensor_tensor(out=xj, in0=xj,
                                  in1=inv_rms[:, None, :].to_broadcast([P, 2, S]), op=ALU.mult)\
                   .then_inc(out_ready, 1)


def blocks_of(w, order):
    w = w.reshape(CHUNKS, CK, P, -1, BLOCK_COLS)[:, :, :, order]
    return w.transpose(3, 0, 2, 1, 4).reshape(len(order) * CHUNKS, P, CHUNK_W)


def kernel(x, w_in, conv_w, pool_w, pool_scale, w_out, norm_mix, norm_mlp, w_up, w_down, norm_final):
    import concourse.bacc as bacc
    from concourse.bass_utils import run_bass_kernel_spmd

    x, w_in, conv_w, pool_w, pool_scale, w_out, norm_mix, norm_mlp, w_up, w_down, norm_final = (
        np.asarray(a) for a in (x, w_in, conv_w, pool_w, pool_scale, w_out, norm_mix, norm_mlp,
                                w_up, w_down, norm_final))

    def tiles(a):
        return a.reshape(-1, P).T

    stream = [blocks_of(w_in[0], [6, 7, 2, 3, 4, 5, 0, 1])]
    stream.append(blocks_of(np.concatenate([w_out[0][D_CONV:], w_out[0][:D_CONV]]), [0, 1, 2, 3]))
    for p in range(PARTS):
        stream.append(blocks_of(w_up[0][:, D * p:D * (p + 1)], [0, 1, 2, 3]))
        stream.append(blocks_of(w_down[0][D * p:D * (p + 1)], [0, 1, 2, 3]))
    edge_inv = np.array([[1.0 / min(t + 1, w) for t in range(EDGE)] for w in WINDOWS], np.float32)
    arrays = {
        "x_t": np.ascontiguousarray(x[0].T.reshape(KT, P, S).transpose(1, 0, 2)),
        "w_stream": np.concatenate(stream),
        "pool_w": np.ascontiguousarray(
            pool_w[0].reshape(len(WINDOWS), 2, P, GROUP).transpose(2, 0, 1, 3).reshape(P, CHUNK_W)),
        "params": np.ascontiguousarray(np.concatenate(
            [tiles(norm_mix[0]), tiles(norm_mlp[0]), tiles(norm_final),
             tiles(conv_w[0][0]), tiles(conv_w[0][1]), tiles(conv_w[0][2]), tiles(pool_scale[0]),
             np.broadcast_to(edge_inv.reshape(1, -1), (P, edge_inv.size))], axis=1)),
    }
    nc = bacc.Bacc("TRN2", target_bir_lowering=False, num_devices=1)
    F32 = mybir.dt.float32
    ins = [nc.dram_tensor(name, a.shape, F32, kind="ExternalInput").ap() for name, a in arrays.items()]
    out = nc.dram_tensor("out", (P, KT, S), F32, kind="ExternalOutput").ap()
    build(nc, *ins, out)
    r = run_bass_kernel_spmd(nc, [arrays], core_ids=[0])
    got = r.results[0]["out"]
    return np.ascontiguousarray(got.transpose(1, 0, 2).reshape(D, S).T).reshape(1, S, D)
```
